# Optimizing a Trainium2 kernel written in Bass

```python
import jax, jax.numpy as jnp
from jax import lax
import numpy as np

D_MODEL = 1024
BATCH = 1
SEQ = 1024
DEPTH = 1

HEAD_DIM = 64
N_ATTN_HEADS = 12
ATTN_WIDTH = N_ATTN_HEADS * HEAD_DIM
CONV_CHANNELS = D_MODEL // 4
MIX_WIDTH = ATTN_WIDTH + CONV_CHANNELS
IN_WIDTH = 3 * ATTN_WIDTH + 2 * CONV_CHANNELS
CONV_WIDTH = 31
DILATED_BRANCHES = ((128, 1), (512, 4), (2048, 16))
ATTN_BLOCK = 128
ROPE_THETA = 500000.0
ROPE_DIM = HEAD_DIM // 4
N_EXPERTS = 32
TOP_K = 4
D_FF = D_MODEL
SWIGLU_LIMIT = 7.0
SWIGLU_ALPHA = 1.702
MOE_BLOCK = 128
PLE_DIM = 256
NORM_EPS = 1e-6

kernel_name = "hymba_dilated_conformer_moe_ple_layer"

def rms_norm(x, g):
    xf = x.astype(jnp.float32)
    y = xf * lax.rsqrt(jnp.mean(xf * xf, axis=-1, keepdims=True) + NORM_EPS)
    return (y * g.astype(jnp.float32)).astype(x.dtype)

def layer_norm(x, g, b):
    xf = x.astype(jnp.float32)
    mu = jnp.mean(xf, axis=-1, keepdims=True)
    var = jnp.mean(jnp.square(xf - mu), axis=-1, keepdims=True)
    y = (xf - mu) * lax.rsqrt(var + NORM_EPS)
    return (y * g.astype(jnp.float32) + b.astype(jnp.float32)).astype(x.dtype)

def partial_rotary(t, positions):
    half = ROPE_DIM // 2
    inv_freq = ROPE_THETA ** (-jnp.arange(0, ROPE_DIM, 2, dtype=jnp.float32) / ROPE_DIM)
    ang = positions.astype(jnp.float32)[..., None] * inv_freq
    cos = jnp.cos(ang)[:, :, None, :]
    sin = jnp.sin(ang)[:, :, None, :]
    tr = t[..., :ROPE_DIM].astype(jnp.float32)
    t1, t2 = tr[..., :half], tr[..., half:]
    rot = jnp.concatenate([t1 * cos - t2 * sin, t2 * cos + t1 * sin], axis=-1)
    return jnp.concatenate([rot.astype(t.dtype), t[..., ROPE_DIM:]], axis=-1)

def banded_causal_attention(q, k, v, window):
    n, length, h, dh = q.shape
    blk = ATTN_BLOCK
    nb = -(-length // blk)
    pad = nb * blk - length
    if pad:
        cfg = ((0, 0), (0, pad), (0, 0), (0, 0))
        q, k, v = jnp.pad(q, cfg), jnp.pad(k, cfg), jnp.pad(v, cfg)
    qb = q.reshape(n, nb, blk, h, dh)
    kb = k.reshape(n, nb, blk, h, dh)
    vb = v.reshape(n, nb, blk, h, dh)
    zk = jnp.zeros_like(kb[:, :1])
    kk = jnp.concatenate([jnp.concatenate([zk, kb[:, :-1]], axis=1), kb], axis=2)
    vv = jnp.concatenate([jnp.concatenate([zk, vb[:, :-1]], axis=1), vb], axis=2)
    s = jnp.einsum('nbqhd,nbkhd->nbhqk', qb, kk, preferred_element_type=jnp.float32)
    s = s * (HEAD_DIM ** -0.5)
    qi = jnp.arange(blk)[:, None]
    kj = jnp.arange(2 * blk)[None, :]
    dist = qi + blk - kj
    bidx = jnp.arange(nb)[:, None, None]
    valid = (dist >= 0) & (dist <= window) & (bidx * blk + kj - blk >= 0)
    s = jnp.where(valid[None, :, None], s, -jnp.inf)
    m = jnp.max(s, axis=-1, keepdims=True)
    e = jnp.exp(s - m)
    den = jnp.sum(e, axis=-1, keepdims=True)
    o = jnp.einsum('nbhqk,nbkhd->nbqhd', (e / den).astype(v.dtype), vv,
                   preferred_element_type=jnp.float32)
    lse = (m + jnp.log(den))[..., 0]
    o = o.reshape(n, nb * blk, h, dh)[:, :length]
    lse = lse.transpose(0, 1, 3, 2).reshape(n, nb * blk, h)[:, :length]
    return o, lse

def dilated_attention(q, k, v):
    b, s, h, dh = q.shape
    outs, lses = [], []
    for window, dil in DILATED_BRANCHES:
        sub = s // dil

        def to_sub(t):
            return t.reshape(b, sub, dil, h, dh).transpose(0, 2, 1, 3, 4).reshape(b * dil, sub, h, dh)

        o, l = banded_causal_attention(to_sub(q), to_sub(k), to_sub(v), window // dil)
        outs.append(o.reshape(b, dil, sub, h, dh).transpose(0, 2, 1, 3, 4).reshape(b, s, h, dh))
        lses.append(l.reshape(b, dil, sub, h).transpose(0, 2, 1, 3).reshape(b, s, h))
    wts = jax.nn.softmax(jnp.stack(lses, axis=0), axis=0)
    return jnp.sum(wts[..., None] * jnp.stack(outs, axis=0), axis=0)

def conformer_conv(c, w_dw, b_dw, g_ln, b_ln):
    a, g = jnp.split(c, 2, axis=-1)
    glu = a * jax.nn.sigmoid(g)
    y = lax.conv_general_dilated(glu, w_dw, window_strides=(1,),
                                 padding=[(CONV_WIDTH - 1, 0)],
                                 dimension_numbers=('NWC', 'WIO', 'NWC'),
                                 feature_group_count=CONV_CHANNELS)
    y = y + b_dw
    y = layer_norm(y, g_ln, b_ln)
    return jax.nn.silu(y)

def moe_ffn(xt, w_router, b_router, w_gate_up, b_gate_up, w_down, b_down):
    t, d = xt.shape
    g = MOE_BLOCK
    logits = (xt @ w_router + b_router).astype(jnp.float32)
    top_val, top_idx = lax.top_k(logits, TOP_K)
    gates = jax.nn.softmax(top_val, axis=-1)
    flat_e = top_idx.reshape(-1)
    flat_tok = jnp.repeat(jnp.arange(t, dtype=jnp.int32), TOP_K)
    flat_g = gates.reshape(-1)
    order = jnp.argsort(flat_e)
    se, stok, sg = flat_e[order], flat_tok[order], flat_g[order]
    counts = jnp.bincount(flat_e, length=N_EXPERTS)
    padded = (counts + g - 1) // g * g
    start = jnp.cumsum(counts) - counts
    pend = jnp.cumsum(padded)
    pstart = pend - padded
    dest = pstart[se] + jnp.arange(t * TOP_K, dtype=jnp.int32) - start[se]
    cap = t * TOP_K + N_EXPERTS * g
    buf_tok = jnp.full((cap,), t, dtype=jnp.int32).at[dest].set(stok)
    buf_g = jnp.zeros((cap,), jnp.float32).at[dest].set(sg)
    n_blk = cap // g
    blk_e = jnp.minimum(jnp.searchsorted(pend, jnp.arange(n_blk) * g, side='right'), N_EXPERTS - 1)
    x_pad = jnp.concatenate([xt, jnp.zeros((1, d), xt.dtype)], axis=0)
    xb = x_pad[buf_tok].reshape(n_blk, g, d)

    def expert_rows(args):
        rows, e = args
        gu = rows @ w_gate_up[e] + b_gate_up[e]
        gate = jnp.minimum(gu[:, :D_FF], SWIGLU_LIMIT)
        up = jnp.clip(gu[:, D_FF:], -SWIGLU_LIMIT, SWIGLU_LIMIT)
        hid = (up + 1.0) * (gate * jax.nn.sigmoid(gate * SWIGLU_ALPHA))
        return hid @ w_down[e] + b_down[e]

    yb = lax.map(expert_rows, (xb, blk_e))
    y = jax.ops.segment_sum(yb.reshape(cap, d).astype(jnp.float32) * buf_g[:, None],
                            buf_tok, num_segments=t + 1)[:t]
    return y.astype(xt.dtype)

def setup_inputs(seed: int = 0) -> dict:
    key = jax.random.key(seed)
    ks = jax.random.split(key, 24)
    f32 = jnp.float32
    nrm = lambda k, shape, scale: jax.random.normal(k, shape, f32) * scale
    gain = lambda k, shape: 1.0 + 0.05 * jax.random.normal(k, shape, f32)
    x = jax.random.normal(ks[0], (BATCH, SEQ, D_MODEL), f32)
    p = jax.random.normal(ks[1], (DEPTH, BATCH, SEQ, PLE_DIM), f32)
    offsets = jax.random.randint(ks[2], (BATCH, 1), 0, 4096, dtype=jnp.int32)
    positions = offsets + jnp.arange(SEQ, dtype=jnp.int32)[None, :]
    return {
        "x": x,
        "p": p,
        "positions": positions,
        "g_mix_pre": gain(ks[3], (DEPTH, D_MODEL)),
        "w_in": nrm(ks[4], (DEPTH, D_MODEL, IN_WIDTH), D_MODEL ** -0.5),
        "w_dw": nrm(ks[5], (DEPTH, CONV_WIDTH, 1, CONV_CHANNELS), CONV_WIDTH ** -0.5),
        "b_dw": nrm(ks[6], (DEPTH, CONV_CHANNELS), 0.01),
        "g_conv_ln": gain(ks[7], (DEPTH, CONV_CHANNELS)),
        "b_conv_ln": nrm(ks[8], (DEPTH, CONV_CHANNELS), 0.01),
        "w_out": nrm(ks[9], (DEPTH, MIX_WIDTH, D_MODEL), MIX_WIDTH ** -0.5),
        "g_mix_post": gain(ks[10], (DEPTH, D_MODEL)),
        "g_ffn_pre": gain(ks[11], (DEPTH, D_MODEL)),
        "w_router": nrm(ks[12], (DEPTH, D_MODEL, N_EXPERTS), D_MODEL ** -0.5),
        "b_router": nrm(ks[13], (DEPTH, N_EXPERTS), 0.01),
        "w_gate_up": nrm(ks[14], (DEPTH, N_EXPERTS, D_MODEL, 2 * D_FF), D_MODEL ** -0.5),
        "b_gate_up": nrm(ks[15], (DEPTH, N_EXPERTS, 2 * D_FF), 0.01),
        "w_down": nrm(ks[16], (DEPTH, N_EXPERTS, D_FF, D_MODEL), D_FF ** -0.5),
        "b_down": nrm(ks[17], (DEPTH, N_EXPERTS, D_MODEL), 0.01),
        "g_ffn_post": gain(ks[18], (DEPTH, D_MODEL)),
        "w_ple": nrm(ks[19], (DEPTH, PLE_DIM, D_MODEL), PLE_DIM ** -0.5),
        "w_ple_gate": nrm(ks[20], (DEPTH, D_MODEL, D_MODEL), D_MODEL ** -0.5),
        "g_ple_post": gain(ks[21], (DEPTH, D_MODEL)),
    }

def reference(x, p, positions, g_mix_pre, w_in, w_dw, b_dw, g_conv_ln, b_conv_ln, w_out,
              g_mix_post, g_ffn_pre, w_router, b_router, w_gate_up, b_gate_up, w_down, b_down,
              g_ffn_post, w_ple, w_ple_gate, g_ple_post):
    b, s, d = x.shape
    h = x
    for i in range(DEPTH):
        u = rms_norm(h, g_mix_pre[i])
        proj = u @ w_in[i]
        q = proj[..., :ATTN_WIDTH].reshape(b, s, N_ATTN_HEADS, HEAD_DIM)
        k = proj[..., ATTN_WIDTH:2 * ATTN_WIDTH].reshape(b, s, N_ATTN_HEADS, HEAD_DIM)
        v = proj[..., 2 * ATTN_WIDTH:3 * ATTN_WIDTH].reshape(b, s, N_ATTN_HEADS, HEAD_DIM)
        c = proj[..., 3 * ATTN_WIDTH:]
        q = partial_rotary(q, positions)
        k = partial_rotary(k, positions)
        attn = dilated_attention(q, k, v).reshape(b, s, ATTN_WIDTH).astype(h.dtype)
        conv = conformer_conv(c, w_dw[i], b_dw[i], g_conv_ln[i], b_conv_ln[i])
        mix = jnp.concatenate([attn, conv.astype(h.dtype)], axis=-1) @ w_out[i]
        h = h + rms_norm(mix, g_mix_post[i])
        u = rms_norm(h, g_ffn_pre[i])
        ffn = moe_ffn(u.reshape(b * s, d), w_router[i], b_router[i], w_gate_up[i],
                      b_gate_up[i], w_down[i], b_down[i]).reshape(b, s, d)
        h = h + rms_norm(ffn, g_ffn_post[i])
        ple = (p[i] @ w_ple[i]) * jax.nn.sigmoid(h @ w_ple_gate[i])
        h = h + rms_norm(ple, g_ple_post[i])
    return h


_drawn_inputs = setup_inputs


def setup_inputs(seed=0):
    import zlib

    import numpy as np

    out = dict(_drawn_inputs(seed))
    spreads = {}
    factors = {'b_gate_up': 8.0, 'b_down': 8.0}
    for name, (base, spread) in spreads.items():
        noise = np.random.default_rng([zlib.crc32(name.encode()), seed]).standard_normal(out[name].shape)
        drawn = base * np.exp(spread * noise) if base else spread * noise
        out[name] = __import__('jax').numpy.asarray(drawn.astype(out[name].dtype))
    for name, factor in factors.items():
        out[name] = (out[name] * factor).astype(out[name].dtype)
    return out
```

```python
from contextlib import ExitStack

import concourse.bass as bass
from concourse import mybir

P = 128
F32 = mybir.dt.float32
F32R = mybir.dt.float32r
I32 = mybir.dt.int32
U32 = mybir.dt.uint32
ALU = mybir.AluOpType
ACT = mybir.ActivationFunctionType

T = 1024
D = 1024
NT = T // P
KD = D // P
HEADS = 12
HD = 64
AW = HEADS * HD
PAIRS = HEADS // 2
CC = 256
TAPS = 31
TAPS_PER_PAIR = (TAPS - 1) // PAIRS
E = 32
TOPK = 4
DFF = 1024
PLE = 256
EPS = 1e-6
LIMIT = 7.0
ALPHA = 1.702
NEG = -1.0e30

BLK = 2 * P
MAX_ITEMS = E + T * TOPK // (BLK + 1)
MAX_BLOCKS = E + T * TOPK // P
PIECES = 12
RAW = 6
SPLIT = 4

TWO_PI = 6.283185307179586
C1 = 6.28125
C2 = 0.0019350051879882812
C3 = TWO_PI - C1 - C2
ROUND = 1.5 * 2.0 ** 23
PI_IN = 3.1415925


class Count:

    def __init__(self, start=0):
        self.start, self.n = start, 0

    def up(self, k=1):
        self.n += k
        return self.start + self.n


def layer(nc, x, p_in, positions, g_mix_pre, w_in, w_dw, b_dw, g_conv_ln, b_conv_ln, w_out, g_mix_post,
          g_ffn_pre, w_router, b_router, w_gate_up, b_gate_up, w_down, b_down, g_ffn_post, w_ple,
          w_ple_gate, g_ple_post, consts, mult_log, out):
    outer = ExitStack()
    with outer:
        stack = [outer]

        def sb(name, shape, dt=F32):
            return stack[-1].enter_context(nc.sbuf_tensor(name, shape, dt))

        def sem(name):
            return outer.enter_context(nc.semaphore(name))

        bank = outer.enter_context(nc.psum_tensor("bank", [P, 8, 512], F32))

        def banks(b, n=1):
            return bank[:, b:b + n, :].rearrange("p b c -> p (b c)")

        h1_dram = nc.dram_tensor("h1_scratch", (T, D), F32, kind="Internal").ap()
        u2_dram = nc.dram_tensor("u2_scratch", (T, D), F32, kind="Internal").ap()
        list_dram = nc.dram_tensor("token_list", (E * T, 1), I32, kind="Internal").ap()
        y_dram = nc.dram_tensor("expert_rows", (MAX_BLOCKS * P, D), F32, kind="Internal").ap()
        bias_dram = nc.dram_tensor("bias_parts", (E, 2, 3 * D), F32, kind="Internal").ap()
        tab_dram = nc.dram_tensor("item_table", (P, 8), I32, kind="Internal").ap()

        cst = sb("cst", [P, 416 + 8])
        ident = cst[:, 0:128]
        rotm = cst[:, 128:256]
        tri = cst[:, 256:384]
        iota_e = cst[:, 384:416]
        freq = cst[:, 416:417]
        pidx = cst[:, 417:418]
        ones = sb("ones", [P, P])
        row_of = sb("row_of", [P, NT, TOPK], I32)
        gate = sb("gate", [P, NT, TOPK])
        tab = sb("tab", [1, P * 8], I32)
        raw = sb("raw", [P, RAW, 4, 512])
        zeros = sb("zeros", [P, 256])

        pre = ExitStack()
        outer.enter_context(pre)
        stack.append(pre)
        xall = sb("xall", [P, NT, D])
        mixT = xall
        uT = sb("uT", [P, KD, T])
        mid = ExitStack()
        pre.enter_context(mid)
        stack.append(mid)
        wqkv = sb("wqkv", [P, 3, KD, P])
        qraw = sb("qraw", [P, T])
        rotc = sb("rotc", [P, T])
        qT = sb("qT", [P, T])
        kT = sb("kT", [P, T])
        vT = sb("vT", [P, T])
        V = sb("V", [P, NT, P])
        S = [sb(f"S{i}", [P, T]) for i in range(3)]
        PT = [sb(f"PT{i}", [P, T]) for i in range(2)]
        mlog = sb("mlog", [P, T])
        cosT = sb("cosT", [P, T])
        sinT = sb("sinT", [P, T])
        glu = sb("glu", [P, 2, TAPS - 1 + T])
        conv = sb("conv", [P, 2, T])
        o_sb = sb("o_sb", [P, 2, P])
        stat = sb("stat", [P, 64])
        gpre = sb("gpre", [P, KD])
        wdw = sb("wdw", [P, 2, TAPS])
        cvec = sb("cvec", [P, 3, 2])
        xn = [qraw, rotc]
        wconv = raw[:, 0:2].rearrange("p a b c -> p (a b c)").rearrange("p (k n) -> p k n", k=KD)
        bias_all = raw[:, 2:4].rearrange("p a b c -> p (a b c)")[0:E, 0:3 * D]
        bias_top = raw[:, 4:6].rearrange("p a b c -> p (a b c)")[0:E, 0:3 * D]
        stack.pop()
        mid.close()

        proj = ExitStack()
        pre.enter_context(proj)
        stack.append(proj)
        wout = uT[:, :, :]
        mixS = [sb(f"mixS{i}", [P, KD, P]) for i in range(2)]
        xr = [sb(f"xr{i}", [P, D]) for i in range(2)]
        h1 = [sb(f"h1_{i}", [P, D]) for i in range(2)]
        u2 = [sb(f"u2_{i}", [P, D]) for i in range(2)]
        u2T = sb("u2T", [P, KD, P])
        junk3 = sb("junk3", [P, D])
        gpost = sb("gpost", [P, D])
        gffn = sb("gffn", [P, D])
        wr = sb("wr", [P, KD, E])
        br = sb("br", [P, E])
        st3 = sb("st3", [P, 2, 8])
        logit = sb("logit", [P, E])
        top = sb("top", [P, NT, 8])
        top8 = sb("top8", [P, 8])
        topi = sb("topi", [P, 8], U32)
        topf = sb("topf", [P, 8])
        hot = sb("hot", [P, TOPK, E])
        M = sb("M", [P, E])
        Macc = sb("Macc", [P, E])
        rank = sb("rank", [P, TOPK])
        rowf = sb("rowf", [P, TOPK])
        row_i = sb("row_i", [P, TOPK], I32)
        tid_f = sb("tid_f", [P, 1])
        tid_i = sb("tid_i", [P, 1], I32)
        junk32 = sb("junk32", [P, TOPK, E])
        zero_i = sb("zero_i", [P, E * T // P], I32)
        cnt = sb("cnt", [P, E])
        npass = sb("npass", [P, E])
        nblk = sb("nblk", [P, E])
        pref = sb("pref", [P, 2, 2, E])
        first = sb("first", [P, E])
        idx_all = sb("idx_all", [P, NT, TOPK])
        rank_all = sb("rank_all", [P, NT, TOPK])
        hot_all = sb("hot_all", [P, NT * TOPK, E])
        item = sb("item", [P, 8])
        item_i = sb("item_i", [P, 8], I32)
        gtmp = sb("gtmp", [P, NT, TOPK])
        gsum = sb("gsum", [P, NT])
        stack.pop()
        proj.close()
        stack.pop()
        pre.close()

        moe = ExitStack()
        outer.enter_context(moe)
        stack.append(moe)
        whi = sb("whi", [P, SPLIT, 4, 512], F32R)
        wlo = sb("wlo", [P, SPLIT, 4, 512], F32R)
        xhi = sb("xhi", [P, 2, KD, P], F32R)
        xlo = sb("xlo", [P, 2, KD, P], F32R)
        hhi = sb("hhi", [P, 2, KD, P], F32R)
        hlo = sb("hlo", [P, 2, KD, P], F32R)
        xg = sb("xg", [P, 2, D])
        ysb = sb("ysb", [P, 2, D])
        gat = sb("gat", [P, 2, 256])
        upc = sb("upc", [P, 2, 256])
        sig = sb("sig", [P, 2, 256])
        hid = sb("hid", [P, 2, 2, 256])
        bsp = sb("bsp", [64, 3 * D], F32R)
        one_r = sb("one_r", [64, P], F32R)
        ids = sb("ids", [P, 2], I32)
        stack.pop()
        moe.close()

        fin = ExitStack()
        outer.enter_context(fin)
        stack.append(fin)
        wpg = raw[:, 0:4].rearrange("p a b c -> p (a b c)").rearrange("p (k n) -> p k n", k=KD)
        wpl = raw[:, 4].rearrange("p b c -> p (b c)").rearrange("p (k n) -> p k n", k=2)
        yg = [sb(f"yg{i}", [P, TOPK, D]) for i in range(2)]
        rsel = sb("rsel", [P, 2, TOPK], I32)
        h2 = [sb(f"h2_{i}", [P, D]) for i in range(2)]
        pt = [sb(f"pt{i}", [P, PLE]) for i in range(2)]
        h2T = sb("h2T", [P, KD, P])
        pT = sb("pT", [P, 2, P])
        sg5 = sb("sg5", [P, D])
        ffn = sb("ffn", [P, D])
        ple = sb("ple", [P, D])
        junk5 = sb("junk5", [P, D])
        gfp = sb("gfp", [P, D])
        gpp = sb("gpp", [P, D])
        st5 = sb("st5", [P, 2, 8])
        stack.pop()
        fin.close()

        tick = sem("tick")
        cst_in = sem("cst_in")
        vec_in = sem("vec_in")
        zeros_set = sem("zeros_set")
        rows_zero = sem("rows_zero")
        taps_in = sem("taps_in")
        x_in = sem("x_in")
        wc_in = sem("wc_in")
        tables_in = sem("tables_in")
        wqkv_in = sem("wqkv_in")
        ones_set = sem("ones_set")
        x_stat = sem("x_stat")
        x_var = sem("x_var")
        x_rstd = sem("x_rstd")
        xn_ready = sem("xn_ready")
        xt_done = sem("xt_done")
        ut_ready = sem("ut_ready")
        glu_pad = sem("glu_pad")
        cproj_done = sem("cproj_done")
        sig_ready = sem("sig_ready")
        glu_ready = sem("glu_ready")
        conv_step = sem("conv_step")
        angle_step = sem("angle_step")
        trig_ready = sem("trig_ready")
        proj_done = sem("proj_done")
        raw_ready = sem("raw_ready")
        rot_done = sem("rot_done")
        cos_part = sem("cos_part")
        rot_step = sem("rot_step")
        qk_ready = sem("qk_ready")
        vt_ready = sem("vt_ready")
        vtr_done = sem("vtr_done")
        v_ready = sem("v_ready")
        s_done = sem("s_done")
        mask_done = sem("mask_done")
        negmax = sem("negmax")
        exp_done = sem("exp_done")
        pt_done = sem("pt_done")
        pt_act = sem("pt_act")
        pt_dve = sem("pt_dve")
        pv_done = sem("pv_done")
        rden_done = sem("rden_done")
        o_ready = sem("o_ready")
        ot_done = sem("ot_done")
        mix_ready = sem("mix_ready")
        ln_dve = sem("ln_dve")
        ln_pe = sem("ln_pe")
        ln_act = sem("ln_act")
        stage2_end = sem("stage2_end")

        wout_in = sem("wout_in")
        vec3_in = sem("vec3_in")
        xr_in = [sem(f"xr_in{i}") for i in range(2)]
        stage_a = sem("stage_a")
        out_done = sem("out_done")
        a3 = sem("a3")
        d3 = sem("d3")
        u2t_done = sem("u2t_done")
        u2t_ready = sem("u2t_ready")
        logit_done = sem("logit_done")
        rank_done = sem("rank_done")
        h1_out = [sem(f"h1_out{i}") for i in range(2)]
        u2_out = [sem(f"u2_out{i}") for i in range(2)]
        list_zero = sem("list_zero")
        zero_set = sem("zero_set")
        ids_out = sem("ids_out")
        e3 = sem("e3")
        cnt_done = sem("cnt_done")
        n2_done = sem("n2_done")
        g3 = sem("g3")
        tab_out = sem("tab_out")
        tab_in = sem("tab_in")
        stage3_end = sem("stage3_end")

        raw_in = [sem(f"raw_in{i}") for i in range(RAW)]
        hi_ready = sem("hi_ready")
        lo_ready = sem("lo_ready")
        w_free = sem("w_free")
        gu_done = sem("gu_done1")
        gu_used = [sem(f"gu_used{b}") for b in range(2)]
        gat_ready = [sem(f"gat_ready{b}") for b in range(2)]
        sig_done = [sem(f"sig_done{b}") for b in range(2)]
        gs_done = [sem(f"gs_done{b}") for b in range(2)]
        hid_ready = [sem(f"hid_ready{b}") for b in range(2)]
        ht_done = [sem(f"ht_done{b}") for b in range(2)]
        hhi_ready = [sem(f"hhi_ready{b}") for b in range(2)]
        hlo_ready = [sem(f"hlo_ready{b}") for b in range(2)]
        y_done = sem("y_done1")
        y_used = [[sem(f"y_used{b}{d}") for d in range(2)] for b in range(2)]
        y_out = [sem(f"y_out{b}") for b in range(2)]
        ids_in = [sem(f"ids_in{b}") for b in range(2)]
        xg_in = [sem(f"xg_in{b}") for b in range(2)]
        xt4_done = [sem(f"xt4_done{b}") for b in range(2)]
        xhi_ready = [sem(f"xhi_ready{b}") for b in range(2)]
        xlo_ready = [sem(f"xlo_ready{b}") for b in range(2)]
        bias_raw_in = sem("bias_raw_in")
        bias_hi = sem("bias_hi")
        bias_lo = sem("bias_lo")
        bias_out = sem("bias_out")
        bias_zero = sem("bias_zero")
        bias_in = [sem(f"bias_in{k}") for k in range(2)]
        bias_used = [sem(f"bias_used{k}") for k in range(2)]
        stage4_end = sem("stage4_end")

        w5_in = sem("w5_in")
        gain5_in = sem("gain5_in")
        rsel_set = sem("rsel_set")
        yg_in = [sem(f"yg_in{i}") for i in range(2)]
        h5_in = [sem(f"h5_in{i}") for i in range(2)]
        ffn_dve = sem("ffn_dve")
        ffn_act = sem("ffn_act")
        ple_dve = sem("ple_dve")
        ple_act = sem("ple_act")
        ple_read = sem("ple_read")
        t5_done = sem("t5_done")
        t5_ready = sem("t5_ready")
        g5_done = sem("g5_done")
        out_dma = [sem(f"out_dma{i}") for i in range(2)]

        block = outer.enter_context(nc.Block())

        EXPERT, ROW, TWO, NTWO, LIVE, BEFORE, START, YROW = range(8)

        def read(eng, n, what):
            hi = {EXPERT: E - 1, ROW: E * T - BLK, TWO: 1, NTWO: MAX_ITEMS, LIVE: 1, BEFORE: MAX_ITEMS,
                  YROW: (MAX_BLOCKS - 2) * P}[what]
            return eng.value_load(tab[0:1, bass.ds(n * 8 + what, 1)], min_val=0, max_val=hi)

        def hold(eng, s, value):
            eng.wait_ge(s, value)
            eng.sem_inc(tick, 1)

        D3 = 30
        F5 = 8
        L5 = 4
        TWO_STEP = 37
        TABLE_STEP = 43

        def col(v, n):
            return v.rearrange("(k p) -> p k", p=P)

        def expert_piece(sp, e, c, slot):
            dst = raw[:, slot]
            if c < 8:
                j, half = c // 2, c % 2
                rows = w_gate_up[0, bass.ds(e, 1), half * 512:half * 512 + 512, :].rearrange(
                    "e (k p) n -> p (e k) n", p=P)
                sp.dma_start(dst[:, :, 0:256], rows[:, :, j * 256:j * 256 + 256]).then_inc(raw_in[slot], 16)
                sp.dma_start(dst[:, :, 256:512],
                             rows[:, :, DFF + j * 256:DFF + j * 256 + 256]).then_inc(raw_in[slot], 16)
            else:
                dcol, half = (c - 8) % 2, (c - 8) // 2
                rows = w_down[0, bass.ds(e, 1), half * 512:half * 512 + 512, :].rearrange(
                    "e (k p) n -> p (e k) n", p=P)
                sp.dma_start(dst, rows[:, :, dcol * 512:dcol * 512 + 512]).then_inc(raw_in[slot], 16)

        def raw_value(n, c):
            first = 32
            second = 32 if c % RAW < 2 else 16
            return n * (first + second) + (first if c < RAW else first + second)

        def pool_fin(pool):
            def fetch5(i, s):
                t = 2 * i + s
                hold(pool, rsel_set, t + 1)
                for k in range(TOPK):
                    pool.indirect_dma_start(out=yg[s][:, k], out_offset=None, in_=y_dram,
                                            in_offset=bass.IndirectOffsetOnAxis(ap=rsel[:, s, k:k + 1], axis=0)
                                            ).then_inc(yg_in[s], 16)
            with pool.Fori(0, NT // 2) as i:
                fetch5(i, 0)
                fetch5(i, 1)

        def experts_pe(pe):
            pe.sem_inc(w_free, SPLIT)
            pe.wait_ge(bias_zero, 2)

            def turn_rows(b, k, before):
                pe.wait_ge(xg_in[b], 16 * k + 16)
                if b == 1:
                    pe.wait_ge(xlo_ready[0], before)
                elif before is not None:
                    pe.wait_ge(xlo_ready[1], before)
                for j in range(KD):
                    mm = pe.transpose(banks(4, 2)[:, j * P:j * P + P], xg[:, b, j * P:j * P + P], ident)
                mm.then_inc(xt4_done[b], 1)

            def turn_hidden(b, j, k):
                pe.wait_ge(hid_ready[b], 4 * k + j + 1)
                pe.wait_ge(hlo_ready[b], 4 * k + j)
                for h in range(2):
                    mm = pe.transpose(banks(6 + b)[:, h * P:h * P + P], hid[:, b, j % 2, h * P:h * P + P], ident)
                mm.then_inc(ht_done[b], 1)

            def products(n, b, c, k):
                if c < 8:
                    q, half, stat_hi, stat_lo = c // 2, c % 2, xhi, xlo
                else:
                    q, half, stat_hi, stat_lo = 4 + (c - 8) % 2, (c - 8) // 2, hhi, hlo
                dst = banks(2 * b + q % 2)
                if half == 0:
                    if q < 2:
                        pe.wait_ge(y_used[b][q], k)
                    else:
                        pe.wait_ge(gu_used[b], 4 * k + q - 1)
                    if q == 0:
                        pe.wait_ge(xlo_ready[b], k + 1)
                    kind = 0 if q < 4 else 1
                    if q in (0, 4):
                        pe.wait_ge(bias_in[kind], 32 * n + 32)
                    mm = pe.matmul(dst, one_r[:], bsp[:, q * 512:q * 512 + 512], start=True, stop=False)
                    if b == 0 and q in (3, 5):
                        mm.then_inc(bias_used[kind], 1)
                if c in (8, 10):
                    pe.wait_ge(hlo_ready[b], 4 * k + (2 if c == 8 else 4))
                s = c % SPLIT
                for j in range(4):
                    if c == 9 and j == 2:
                        turn_hidden(b, 3, k)
                    kt = half * 4 + j
                    last = half == 1 and j == 3
                    pe.matmul(dst, stat_hi[:, b, kt], whi[:, s, j], start=False, stop=False)
                    pe.matmul(dst, stat_lo[:, b, kt], whi[:, s, j], start=False, stop=False)
                    mm = pe.matmul(dst, stat_hi[:, b, kt], wlo[:, s, j], start=False, stop=last)
                return mm

            turn_rows(0, 0, None)
            with pe.If(read(pe, 0, TWO) > 0):
                turn_rows(1, 0, 1)
            with pe.Fori(0, MAX_ITEMS) as n:
                with pe.If(read(pe, n, LIVE) > 0):
                    two = read(pe, n, TWO)
                    k1 = read(pe, n, NTWO)
                    nxt = read(pe, n + 1, LIVE)
                    nxt2 = read(pe, n + 1, TWO)
                    nk1 = read(pe, n + 1, NTWO)
                    for c in range(PIECES):
                        pe.wait_ge(lo_ready, PIECES * n + c + 1)
                        with pe.If(two > 0):
                            mm = products(n, 1, c, k1)
                            if c in (1, 3, 5, 7):
                                mm.then_inc(gu_done, 1)
                            if c in (10, 11):
                                mm.then_inc(y_done, 1)
                            if c in (3, 5, 7):
                                turn_hidden(1, (c - 3) // 2, k1)
                        mm = products(n, 0, c, n)
                        mm.then_inc(w_free, 1)
                        if c in (3, 5, 7):
                            turn_hidden(0, (c - 3) // 2, n)
                        if c == 7:
                            with pe.If(nxt > 0):
                                turn_rows(0, n + 1, nk1)
                        if c == 9:
                            with pe.If(nxt2 > 0):
                                turn_rows(1, nk1, n + 2)
            pe.transpose(banks(7)[:, 0:P], ident, ident).then_inc(stage4_end, 1)
            pe.wait_ge(stage4_end, 4)

        def out_pe(pe):
            pe.wait_ge(w5_in, 32)

            def turn5(i, s):
                t = 2 * i + s
                pe.wait_ge(ffn_dve, F5 * t + F5)
                for k in range(KD):
                    pe.transpose(banks(0, 2)[:, k * P:k * P + P], h2[s][:, k * P:k * P + P], ident)
                for k in range(2):
                    mm = pe.transpose(banks(2)[:, k * P:k * P + P], pt[s][:, k * P:k * P + P], ident)
                mm.then_inc(t5_done, 1)
                pe.wait_ge(t5_ready, 2 * t + 2)
                pe.wait_ge(ple_read, t)
                for half in range(2):
                    for k in range(KD):
                        pe.matmul(banks(4 + half), h2T[:, k], wpg[:, k, half * 512:half * 512 + 512],
                                  start=(k == 0), stop=(k == KD - 1))
                    for k in range(2):
                        mm = pe.matmul(banks(6 + half), pT[:, k], wpl[:, k, half * 512:half * 512 + 512],
                                       start=(k == 0), stop=(k == 1))
                mm.then_inc(g5_done, 1)

            with pe.Fori(0, NT // 2) as i:
                turn5(i, 0)
                turn5(i, 1)

        def act_fin(act):
            act.activation(ysb[:, 0, 0:1], ysb[:, 0, 1:2], ACT.Copy).then_inc(stage4_end, 1)
            act.wait_ge(stage4_end, 4)

            def ffn_part(i, s):
                t = 2 * i + s
                act.wait_ge(ffn_act, 2 * t)
                act.wait_ge(ffn_dve, F5 * t + 4)
                act.activation(junk5[:], ffn[:], ACT.Square, accum_out=st5[:, s, 0:1]).then_inc(ffn_act, 1)
                act.wait_ge(ffn_dve, F5 * t + 6)
                act.activation(st5[:, s, 2:3], st5[:, s, 1:2], ACT.Sqrt).then_inc(ffn_act, 1)

            def columns5(i, s):
                act.wait_ge(t5_done, 2 * i + s + 1)
                act.activation(h2T[:].rearrange("p k n -> p (k n)"), banks(0, 2), ACT.Copy).then_inc(t5_ready, 1)
                act.activation(pT[:].rearrange("p k n -> p (k n)"), banks(2)[:, 0:2 * P], ACT.Copy).then_inc(t5_ready, 1)

            def gates5(i, s):
                t = 2 * i + s
                act.wait_ge(g5_done, t + 1)
                act.wait_ge(ple_act, 3 * t)
                act.activation(sg5[:], banks(4, 2), ACT.Sigmoid).then_inc(ple_act, 1)

            def ple_part(i, s):
                t = 2 * i + s
                act.wait_ge(ple_read, t + 1)
                act.activation(sg5[:], ple[:], ACT.Square, accum_out=st5[:, s, 3:4]).then_inc(ple_act, 1)
                act.wait_ge(ple_dve, L5 * t + 2)
                act.activation(st5[:, s, 5:6], st5[:, s, 4:5], ACT.Sqrt).then_inc(ple_act, 1)

            def two_tiles(i, s, j, r):
                ffn_part(j, r)
                gates5(i, s)
                columns5(j, r)
                ple_part(i, s)

            ffn_part(0, 0)
            columns5(0, 0)
            with act.Fori(0, NT // 2 - 1) as i:
                two_tiles(i, 0, i, 1)
                two_tiles(i, 1, i + 1, 0)
            two_tiles(NT // 2 - 1, 0, NT // 2 - 1, 1)
            gates5(NT // 2 - 1, 1)
            ple_part(NT // 2 - 1, 1)

        def experts_dve(dve):
            def split_lo(n, c):
                dve.wait_ge(hi_ready, PIECES * n + c + 1)
                dve.tensor_tensor(wlo[:, c % SPLIT], raw[:, c % RAW], whi[:, c % SPLIT].bitcast(F32),
                                  ALU.subtract).then_inc(lo_ready, 1)

            def columns(b, k):
                dve.wait_ge(xhi_ready[b], k + 1)
                dve.tensor_tensor(xlo[:, b].rearrange("p k n -> p (k n)"), banks(4, 2),
                                  xhi[:, b].rearrange("p k n -> p (k n)").bitcast(F32),
                                  ALU.subtract).then_inc(xlo_ready[b], 1)

            def clamp(b, j, k):
                if b == 1:
                    dve.wait_ge(gu_done, 4 * k + j + 1)
                else:
                    dve.wait_ge(w_free, PIECES * k + SPLIT + 2 * j + 2)
                src = banks(2 * b + j % 2)
                dve.wait_ge(hid_ready[b], 4 * k + j)
                dve.tensor_scalar(gat[:, b], src[:, 0:256], LIMIT, None, ALU.min).then_inc(gat_ready[b], 1)
                dve.tensor_scalar(upc[:, b], src[:, 256:512], LIMIT, -LIMIT, ALU.min, ALU.max).then_inc(gu_used[b], 1)

            def gated(b, j, k):
                dve.wait_ge(sig_done[b], 4 * k + j + 1)
                dve.tensor_tensor(sig[:, b], gat[:, b], sig[:, b], ALU.mult).then_inc(gs_done[b], 1)
                dve.wait_ge(gs_done[b], 4 * k + j + 1)
                if j >= 2:
                    dve.wait_ge(ht_done[b], 4 * k + j - 1)
                else:
                    dve.wait_ge(ht_done[b], 4 * k)
                dve.scalar_tensor_tensor(out=hid[:, b, j % 2], in0=upc[:, b], scalar=1.0, in1=sig[:, b],
                                         op0=ALU.add, op1=ALU.mult).then_inc(hid_ready[b], 1)

            def hidden(b, j, k):
                dve.wait_ge(hhi_ready[b], 4 * k + j + 1)
                dve.tensor_tensor(hlo[:, b, 2 * j:2 * j + 2].rearrange("p k n -> p (k n)"), banks(6 + b)[:, 0:256],
                                  hhi[:, b, 2 * j:2 * j + 2].rearrange("p k n -> p (k n)").bitcast(F32),
                                  ALU.subtract).then_inc(hlo_ready[b], 1)

            for c in range(SPLIT):
                split_lo(0, c)
            columns(0, 0)
            with dve.If(read(dve, 0, TWO) > 0):
                columns(1, 0)
            with dve.Fori(0, MAX_ITEMS) as n:
                with dve.If(read(dve, n, LIVE) > 0):
                    two = read(dve, n, TWO)
                    k1 = read(dve, n, NTWO)
                    nxt = read(dve, n + 1, LIVE)
                    nxt2 = read(dve, n + 1, TWO)
                    nk1 = read(dve, n + 1, NTWO)
                    for c in range(PIECES):
                        j = (c - 1) // 2
                        if c in (1, 3, 5, 7):
                            with dve.If(two > 0):
                                clamp(1, j, k1)
                            clamp(0, j, n)
                            with dve.If(two > 0):
                                gated(1, j, k1)
                            gated(0, j, n)
                        if c in (4, 6, 8, 9):
                            with dve.If(two > 0):
                                hidden(1, (c - 3) // 2, k1)
                            hidden(0, (c - 3) // 2, n)
                        if c + SPLIT < PIECES:
                            split_lo(n, c + SPLIT)
                        else:
                            if c == 10:
                                with dve.If(nxt2 > 0):
                                    columns(1, nk1)
                            with dve.If(nxt > 0):
                                if c == 8:
                                    columns(0, n + 1)
                                split_lo(n + 1, c + SPLIT - PIECES)
            dve.memset(gat[:, 0, 0:1], 0.0).then_inc(stage4_end, 1)
            dve.wait_ge(stage4_end, 4)

        def out_dve(dve):
            def pick(i, s):
                t = 2 * i + s
                dve.tensor_copy(rsel[:, s], row_of[:, bass.ds(t, 1)].rearrange("p t k -> p (t k)")).then_inc(rsel_set, 1)

            def ffn_part(i, s, following=True):
                t = 2 * i + s
                n = Count(F5 * t)
                dve.wait_ge(ffn_dve, n.up(0))
                dve.wait_ge(yg_in[s], 16 * TOPK * (i + 1))
                gt = gate[:, bass.ds(t, 1)].rearrange("p t k -> p (t k)")
                dve.tensor_scalar(ffn[:], yg[s][:, 0], gt[:, 0:1], None, ALU.mult).then_inc(ffn_dve, 1)
                dve.wait_ge(ffn_dve, n.up())
                for k in range(1, TOPK):
                    dve.scalar_tensor_tensor(out=ffn[:], in0=yg[s][:, k], scalar=gt[:, k:k + 1], in1=ffn[:],
                                             op0=ALU.mult, op1=ALU.add).then_inc(ffn_dve, 1)
                    dve.wait_ge(ffn_dve, n.up())
                if following:
                    pick(i + 1, s)
                dve.wait_ge(ffn_act, 2 * t + 1)
                dve.tensor_scalar(st5[:, s, 1:2], st5[:, s, 0:1], 1.0 / D, EPS, ALU.mult, ALU.add).then_inc(ffn_dve, 1)
                dve.wait_ge(ffn_dve, n.up())
                dve.reciprocal(st5[:, s, 1:2], st5[:, s, 1:2]).then_inc(ffn_dve, 1)
                n.up()
                dve.wait_ge(ffn_act, 2 * t + 2)
                dve.scalar_tensor_tensor(out=ffn[:], in0=ffn[:], scalar=st5[:, s, 2:3], in1=gfp[:],
                                         op0=ALU.mult, op1=ALU.mult).then_inc(ffn_dve, 1)
                dve.wait_ge(ffn_dve, n.up())
                dve.wait_ge(h5_in[s], 32 * i + 32)
                dve.tensor_tensor(h2[s][:], h2[s][:], ffn[:], ALU.add).then_inc(ffn_dve, 1)
                n.up()
                assert n.n == F5, n.n

            def ple_part(i, s):
                t = 2 * i + s
                n = Count(L5 * t)
                dve.wait_ge(ple_act, 3 * t + 1)
                dve.wait_ge(ple_dve, n.up(0))
                dve.tensor_tensor(ple[:], banks(6, 2), sg5[:], ALU.mult).then_inc(ple_read, 1)
                dve.wait_ge(ple_act, 3 * t + 2)
                dve.tensor_scalar(st5[:, s, 4:5], st5[:, s, 3:4], 1.0 / D, EPS, ALU.mult, ALU.add).then_inc(ple_dve, 1)
                dve.wait_ge(ple_dve, n.up())
                dve.reciprocal(st5[:, s, 4:5], st5[:, s, 4:5]).then_inc(ple_dve, 1)
                n.up()
                dve.wait_ge(ple_act, 3 * t + 3)
                dve.scalar_tensor_tensor(out=ple[:], in0=ple[:], scalar=st5[:, s, 5:6], in1=gpp[:],
                                         op0=ALU.mult, op1=ALU.mult).then_inc(ple_dve, 1)
                dve.wait_ge(ple_dve, n.up())
                dve.tensor_tensor(h2[s][:], h2[s][:], ple[:], ALU.add).then_inc(ple_dve, 1)
                n.up()
                assert n.n == L5, n.n

            pick(0, 0)
            pick(0, 1)
            dve.wait_ge(gain5_in, 32)
            ffn_part(0, 0)

            def pair5(i, following=True):
                ffn_part(i, 1)
                ple_part(i, 0)
                ffn_part(i + 1, 0, following)
                ple_part(i, 1)

            with dve.Fori(0, NT // 2 - 2) as i:
                pair5(i)
            pair5(NT // 2 - 2, False)
            ffn_part(NT // 2 - 1, 1, False)
            ple_part(NT // 2 - 1, 0)
            ple_part(NT // 2 - 1, 1)

        @block.sync
        def _(sp):
            sp.dma_start(cst[:], consts).then_inc(cst_in, 16)
            sp.dma_start(xall[:], x[0].rearrange("(t p) d -> p t d", p=P)).then_inc(x_in, 16)
            sp.dma_start(wconv, w_in[0, :, 3 * AW:].rearrange("(k p) n -> p k n", p=P)).then_inc(wc_in, 16)
            for m in range(3):
                sp.dma_start(wqkv[:, m], w_in[0, :, m * AW:m * AW + P].rearrange(
                    "(k p) n -> p k n", p=P)).then_inc(wqkv_in, 16)
            sp.dma_start(mlog[:], mult_log).then_inc(tables_in, 16)
            for h in range(2):
                sp.dma_start(bias_all[:, 0:2 * DFF].rearrange("e (j h n) -> e h j n", h=2, n=256)[:, h],
                             b_gate_up[0, :, h * DFF:h * DFF + DFF].rearrange("e (j n) -> e j n", n=256)
                             ).then_inc(bias_raw_in, 16)
            sp.dma_start(bias_all[:, 2 * DFF:3 * DFF], b_down[0]).then_inc(bias_raw_in, 16)
            with sp.Fori(1, PAIRS) as g:
                for m in range(3):
                    sp.wait_ge(proj_done, 3 * g - 2 + m)
                    sp.dma_start(wqkv[:, m], w_in[0, :, bass.ds(m * AW + g * P, P)].rearrange(
                        "(k p) n -> p k n", p=P)).then_inc(wqkv_in, 16)
            sp.wait_ge(bias_hi, 1)
            sp.dma_start(bias_dram[:, 0, :], bias_top).then_inc(bias_out, 16)
            sp.wait_ge(bias_lo, 1)
            sp.dma_start(bias_dram[:, 1, :], bias_all).then_inc(bias_out, 16)
            sp.wait_ge(bias_out, 32)
            sp.wait_ge(cproj_done, 2)
            for c in range(RAW):
                expert_piece(sp, 0, c, c)
            sp.wait_ge(proj_done, 3 * PAIRS)
            sp.dma_start(wout, w_out[0].rearrange("(k p) n -> p k n", p=P)).then_inc(wout_in, 16)
            sp.wait_ge(stage2_end, 4)
            sp.dma_start(wr[:], w_router[0].rearrange("(k p) n -> p k n", p=P)).then_inc(vec3_in, 16)
            sp.dma_start(br[:], b_router[0].partition_broadcast(P)).then_inc(vec3_in, 16)
            sp.dma_start(gpost[:], g_mix_post[0].partition_broadcast(P)).then_inc(vec3_in, 16)
            sp.dma_start(gffn[:], g_ffn_pre[0].partition_broadcast(P)).then_inc(vec3_in, 16)
            for s in range(2):
                sp.dma_start(xr[s][:], x[0, s * P:s * P + P, :]).then_inc(xr_in[s], 16)
            sp.wait_ge(zero_set, 1)
            sp.dma_start(list_dram.rearrange("(p n) o -> p (n o)", p=P), zero_i[:]).then_inc(list_zero, 16)

            def store3(i, s):
                t = 2 * i + s
                sp.wait_ge(d3, D3 * t + 4)
                sp.dma_start(h1_dram[bass.ds(t * P, P), :], h1[s][:]).then_inc(h1_out[s], 16)
                sp.wait_ge(d3, D3 * t + 7)
                sp.dma_start(u2_dram[bass.ds(t * P, P), :], u2[s][:]).then_inc(u2_out[s], 16)

            with sp.Fori(0, NT // 2 - 1) as i:
                for s in range(2):
                    store3(i, s)
                    sp.dma_start(xr[s][:], x[0, bass.ds((2 * i + s + 2) * P, P), :]).then_inc(xr_in[s], 16)
            for s in range(2):
                store3(NT // 2 - 1, s)
            for s in range(2):
                sp.wait_ge(h1_out[s], 16 * NT // 2)
                sp.wait_ge(u2_out[s], 16 * NT // 2)
            sp.wait_ge(e3, TABLE_STEP)
            sp.dma_start(tab_dram, item_i[:]).then_inc(tab_out, 16)
            sp.wait_ge(tab_out, 16)
            sp.dma_start(tab[:], tab_dram.rearrange("(o p) c -> o (p c)", o=1)).then_inc(tab_in, 16)
            sp.wait_ge(tab_in, 16)
            sp.wait_ge(stage3_end, 4)

            def bias_rows(e, k):
                lo, hi = (0, 2 * DFF) if k == 0 else (2 * DFF, 3 * DFF)
                for part in range(2):
                    sp.dma_start(bsp[32 * part:32 * part + 1, lo:hi].bitcast(F32),
                                 bias_dram[bass.ds(e, 1), part, lo:hi]).then_inc(bias_in[k], 16)

            sp.wait_ge(bias_zero, 2)
            for k in range(2):
                bias_rows(0, k)
            with sp.Fori(0, MAX_ITEMS) as n:
                with sp.If(read(sp, n, LIVE) > 0):
                    e = read(sp, n, EXPERT)
                    for c in range(RAW, PIECES):
                        sp.wait_ge(lo_ready, PIECES * n + c - RAW + 1)
                        expert_piece(sp, e, c, c % RAW)
                with sp.If(read(sp, n + 1, LIVE) > 0):
                    e = read(sp, n + 1, EXPERT)
                    for c in range(RAW):
                        sp.wait_ge(lo_ready, PIECES * n + RAW + c + 1)
                        expert_piece(sp, e, c, c)
                        if c in (3, 5):
                            sp.wait_ge(bias_used[c // 4], n + 1)
                            bias_rows(e, c // 4)
            sp.wait_ge(lo_ready, read(sp, P - 1, BEFORE) * PIECES)
            sp.dma_start(wpg[:], w_ple_gate[0].rearrange("(k p) n -> p k n", p=P)).then_inc(w5_in, 16)
            sp.dma_start(wpl[:], w_ple[0].rearrange("(k p) n -> p k n", p=P)).then_inc(w5_in, 16)
            sp.wait_ge(stage4_end, 4)
            sp.dma_start(gfp[:], g_ffn_post[0].partition_broadcast(P)).then_inc(gain5_in, 16)
            sp.dma_start(gpp[:], g_ple_post[0].partition_broadcast(P)).then_inc(gain5_in, 16)

            def load5(i, s):
                t = 2 * i + s
                sp.dma_start(h2[s][:], h1_dram[bass.ds(t * P, P), :]).then_inc(h5_in[s], 16)
                sp.dma_start(pt[s][:], p_in[0, 0, bass.ds(t * P, P), :]).then_inc(h5_in[s], 16)

            def store5(i, s):
                t = 2 * i + s
                sp.wait_ge(ple_dve, L5 * t + L5)
                sp.dma_start(out[0, bass.ds(t * P, P), :], h2[s][:]).then_inc(out_dma[s], 16)

            load5(0, 0)
            load5(0, 1)
            with sp.Fori(0, NT // 2 - 1) as i:
                for s in range(2):
                    store5(i, s)
                    sp.wait_ge(out_dma[s], 16 * i + 16)
                    load5(i + 1, s)
            for s in range(2):
                store5(NT // 2 - 1, s)
            for s in range(2):
                sp.wait_ge(out_dma[s], 16 * NT // 2)

        @block.gpsimd
        def _(pool):
            pool.memset(zeros[:], 0.0).then_inc(zeros_set, 1)
            pool.memset(ones[:], 1.0).then_inc(ones_set, 1)
            pool.memset(glu[:, :, 0:TAPS - 1], 0.0).then_inc(glu_pad, 1)
            pool.dma_start(gpre[:], col(g_mix_pre[0], KD), allow_slow_non_contiguous=True).then_inc(vec_in, 16)
            pool.dma_start(S[0][:].bitcast(I32), positions[0].partition_broadcast(P)).then_inc(vec_in, 16)
            for k, v in enumerate((b_dw, g_conv_ln, b_conv_ln)):
                pool.dma_start(cvec[:, k], col(v[0], 2), allow_slow_non_contiguous=True).then_inc(taps_in, 16)
            for c in range(2):
                pool.dma_start(wdw[:, c], w_dw[0, :, 0, c * P:c * P + P].rearrange("k p -> p k"),
                               allow_slow_non_contiguous=True).then_inc(taps_in, 16)
            pool.wait_ge(trig_ready, 2)
            with pool.Fori(0, PAIRS) as g:
                for m in range(2):
                    pool.wait_ge(raw_ready, 2 * g + m + 1)
                    pool.wait_ge(qk_ready, 2 * g + m)
                    pool.tensor_tensor(rotc[:], qraw[:], cosT[:], ALU.mult).then_inc(cos_part, 1)
            pool.wait_ge(qk_ready, 2 * PAIRS)
            pool.wait_ge(mix_ready, NT * PAIRS)
            pool.memset(o_sb[:, 0, 0:1], 0.0).then_inc(stage2_end, 1)
            pool.wait_ge(stage2_end, 4)
            pool.memset(zero_i[:], 0).then_inc(zero_set, 1)
            pool.wait_ge(list_zero, 16)
            with pool.Fori(0, NT) as t:
                hold(pool, d3, D3 * t + D3)
                for k in range(TOPK):
                    pool.indirect_dma_start(out=list_dram, out_offset=bass.IndirectOffsetOnAxis(
                        ap=row_i[:, k:k + 1], axis=0), in_=tid_i[:], in_offset=None).then_inc(ids_out, 16)
            pool.wait_ge(ids_out, 16 * TOPK * NT)
            pool.memset(zero_i[:, 0:1], 0).then_inc(stage3_end, 1)
            pool.wait_ge(stage3_end, 4)
            pool.wait_ge(tab_in, 16)
            for s in range(2):
                pool.wait_ge(u2_out[s], 16 * NT // 2)

            pool.memset(one_r[:].bitcast(F32), 1.0).then_inc(bias_zero, 1)
            pool.memset(bsp[:].bitcast(F32), 0.0).then_inc(bias_zero, 1)
            pool.wait_ge(bias_zero, 2)

            def fetch_rows(n, b, k):
                row = read(pool, n, ROW) + b * P
                pool.wait_ge(xt4_done[b], k)
                pool.dma_start(ids[:, b:b + 1], list_dram[bass.ds(row, P), :]).then_inc(ids_in[b], 16)
                hold(pool, ids_in[b], 16 * k + 16)
                pool.indirect_dma_start(out=xg[:, b], out_offset=None, in_=u2_dram,
                                        in_offset=bass.IndirectOffsetOnAxis(ap=ids[:, b:b + 1], axis=0)
                                        ).then_inc(xg_in[b], 16)

            def prepare(n):
                fetch_rows(n, 0, n)
                with pool.If(read(pool, n, TWO) > 0):
                    fetch_rows(n, 1, read(pool, n, NTWO))

            prepare(0)
            with pool.Fori(0, MAX_ITEMS) as n:
                with pool.If(read(pool, n + 1, LIVE) > 0):
                    prepare(n + 1)
            pool.wait_ge(stage4_end, 3)
            pool.memset(ids[:], 0).then_inc(stage4_end, 1)
            pool.wait_ge(stage4_end, 4)
            pool_fin(pool)

        @block.tensor
        def _(pe):
            pe.wait_ge(cst_in, 16)

            def turn_x(i, s):
                t = 2 * i + s
                pe.wait_ge(xn_ready, t + 1)
                pe.wait_ge(ut_ready, t - 1) if not (isinstance(i, int) and i == 0) else None
                for k in range(KD):
                    mm = pe.transpose(banks(2 * s, 2)[:, k * P:k * P + P], xn[s][:, k * P:k * P + P], ident)
                mm.then_inc(xt_done, 1)

            turn_x(0, 0)
            turn_x(0, 1)
            with pe.Fori(1, NT // 2) as i:
                turn_x(i, 0)
                turn_x(i, 1)

            def project(w, m, first_bank):
                for half in range(2):
                    for k in range(KD):
                        mm = pe.matmul(banks(first_bank + half), w(k, m), uT[:, k, half * 512:half * 512 + 512],
                                       start=(k == 0), stop=(k == KD - 1))
                return mm

            pe.wait_ge(ut_ready, NT)
            pe.wait_ge(wc_in, 16)
            for c in range(2):
                project(lambda k, m: wconv[:, k, m * P:m * P + P], c, 4 * c)
                project(lambda k, m: wconv[:, k, m * P:m * P + P], 2 + c, 4 * c + 2).then_inc(cproj_done, 1)
            pe.wait_ge(glu_ready, 2)
            pe.wait_ge(trig_ready, 2)

            def scores(g, u):
                i, hd = u // 2, u % 2
                if u >= 2:
                    pe.wait_ge(mask_done, 16 * g + u - 1)
                n = (i + 1) * P
                r = slice(hd * HD, hd * HD + HD)
                for c in range(0, n, 512):
                    w = min(512, n - c)
                    mm = pe.matmul(banks(2 * (u % 2) + c // 512)[:, 0:w], qT[r, i * P:i * P + P], kT[r, c:c + w],
                                   start=True, stop=True)
                mm.then_inc(s_done, 1)

            def turn_probs(g, u):
                i = u // 2
                pe.wait_ge(exp_done, 16 * g + u + 1)
                if u >= 1:
                    pe.wait_ge(pt_act, 16 * g + u)
                if u >= 9:
                    pe.wait_ge(pt_dve, 8 * g + u - 8)
                for k in range(i + 1):
                    mm = pe.transpose(banks(4, 2)[:, k * P:k * P + P], S[u % 3][:, k * P:k * P + P], ident)
                mm.then_inc(pt_done, 1)

            def values(g, u):
                i, hd = u // 2, u % 2
                pe.wait_ge(pt_act, 16 * g + u + 1)
                if u >= 8:
                    pe.wait_ge(pt_dve, 8 * g + u - 7)
                pe.wait_ge(o_ready, 16 * g + u)
                for k in range(i + 1):
                    mm = pe.matmul(banks(6)[:, 0:HD], PT[u % 2][:, k * P:k * P + P], V[:, k, hd * HD:hd * HD + HD],
                                   start=(k == 0), stop=(k == i))
                mm.then_inc(pv_done, 1)

            def turn_out(g, i):
                pe.wait_ge(o_ready, 16 * g + 2 * i + 2)
                pe.wait_ge(mix_ready, NT * g + i)
                pe.transpose(banks(7)[:, 0:P], o_sb[:, i % 2], ident).then_inc(ot_done, 1)

            with pe.Fori(0, PAIRS) as g:
                for m in range(3):
                    pe.wait_ge(wqkv_in, 48 * g + 48)
                    if m == 2:
                        pe.wait_ge(pt_act, 16 * g)
                        pe.wait_ge(pt_dve, 8 * g)
                    else:
                        pe.wait_ge(mask_done, 16 * g)
                    project(lambda k, m: wqkv[:, m, k, :], m, 2 * m).then_inc(proj_done, 1)
                pe.wait_ge(o_ready, 16 * g)
                pe.wait_ge(mix_ready, NT * g)
                for m in range(2):
                    pe.wait_ge(raw_ready, 2 * g + m + 1)
                    b = 6 if m == 0 else 0
                    for half in range(2):
                        mm = pe.matmul(banks(b + half), rotm, qraw[:, half * 512:half * 512 + 512],
                                       start=True, stop=True)
                    mm.then_inc(rot_done, 1)
                pe.wait_ge(vt_ready, g + 1)
                for k in range(NT):
                    mm = pe.transpose(banks(2, 2)[:, k * P:k * P + P], vT[:, k * P:k * P + P], ident)
                mm.then_inc(vtr_done, 1)
                pe.wait_ge(qk_ready, 2 * g + 2)
                pe.wait_ge(v_ready, g + 1)
                scores(g, 0)
                scores(g, 1)
                for u in range(16):
                    if u + 2 < 16:
                        scores(g, u + 2)
                    turn_probs(g, u)
                    if u >= 1:
                        values(g, u - 1)
                    if u >= 4 and u % 2 == 0:
                        turn_out(g, u // 2 - 2)
                values(g, 15)
                turn_out(g, 6)
                turn_out(g, 7)

            for r in range(2):
                pe.wait_ge(ln_dve, 1) if r == 0 else pe.wait_ge(ln_act, 2)
                if r == 0:
                    pe.wait_ge(mix_ready, NT * PAIRS)
                for half in range(2):
                    for c in range(2):
                        src = conv[:, c, half * 512:half * 512 + 512] if r == 0 else S[c][:, half * 512:half * 512 + 512]
                        mm = pe.matmul(banks(2 * r + half), ones[:], src, start=(c == 0), stop=(c == 1))
                mm.then_inc(ln_pe, 1)
            pe.transpose(banks(7)[:, 0:P], ident, ident).then_inc(stage2_end, 1)
            pe.wait_ge(stage2_end, 4)

            pe.wait_ge(wout_in, 16)
            pe.wait_ge(vec3_in, 64)

            def out_proj(i, s):
                t = 2 * i + s
                pe.wait_ge(stage_a, t + 1)
                if not (isinstance(i, int) and i == 0):
                    pe.wait_ge(d3, D3 * (t - 2) + 3)
                for half in range(2):
                    for k in range(KD):
                        mm = pe.matmul(banks(2 * s + half), mixS[s][:, k], wout[:, k, half * 512:half * 512 + 512],
                                       start=(k == 0), stop=(k == KD - 1))
                mm.then_inc(out_done, 1)

            def route(i, s):
                t = 2 * i + s
                pe.wait_ge(d3, D3 * t + 7)
                for k in range(KD):
                    mm = pe.transpose(banks(4, 2)[:, k * P:k * P + P], u2[s][:, k * P:k * P + P], ident)
                mm.then_inc(u2t_done, 1)
                pe.wait_ge(u2t_ready, t + 1)
                for k in range(KD):
                    mm = pe.matmul(banks(6)[:, 0:E], u2T[:, k], wr[:, k], start=(k == 0), stop=(k == KD - 1))
                mm.then_inc(logit_done, 1)
                pe.wait_ge(d3, D3 * t + 17)
                pe.matmul(banks(7)[:, 0:E], tri, M[:], start=True, stop=False)
                pe.matmul(banks(7)[:, 0:E], ones[:], Macc[:], start=False, stop=True).then_inc(rank_done, 1)

            out_proj(0, 0)
            out_proj(0, 1)
            with pe.Fori(0, NT // 2 - 1) as i:
                route(i, 0)
                out_proj(i + 1, 0)
                route(i, 1)
                out_proj(i + 1, 1)
            route(NT // 2 - 1, 0)
            route(NT // 2 - 1, 1)
            pe.wait_ge(d3, D3 * NT)
            pe.matmul(banks(0)[:, 0:E], ones[:], Macc[:], start=True, stop=True).then_inc(cnt_done, 1)
            pe.wait_ge(e3, TWO_STEP)
            pe.matmul(banks(1)[:, 0:1], tri, item[:, TWO:TWO + 1], start=True, stop=True).then_inc(n2_done, 1)
            pe.transpose(banks(7)[:, 0:P], ident, ident).then_inc(stage3_end, 1)
            pe.wait_ge(stage3_end, 4)
            pe.wait_ge(tab_in, 16)
            experts_pe(pe)
            out_pe(pe)

        @block.scalar
        def _(act):
            act.wait_ge(x_in, 16)
            with act.Fori(0, NT) as t:
                act.wait_ge(x_stat, t)
                act.activation(PT[0][:], xall[:, bass.ds(t, 1)].rearrange("p t d -> p (t d)"), ACT.Square,
                               accum_out=stat[:, bass.ds(t, 1)]).then_inc(x_stat, 1)
            act.wait_ge(x_var, 2)
            act.activation(stat[:, 8:16], stat[:, 16:24], ACT.Sqrt).then_inc(x_rstd, 1)
            act.wait_ge(x_rstd, 1)

            def scale_x(i, s, first=False):
                t = 2 * i + s
                if not first:
                    act.wait_ge(xt_done, t - 1)
                act.activation(xn[s][:], xall[:, bass.ds(t, 1)].rearrange("p t d -> p (t d)"), ACT.Copy,
                               scale=stat[:, bass.ds(8 + t, 1)]).then_inc(xn_ready, 1)

            scale_x(0, 0, True)
            scale_x(0, 1, True)
            with act.Fori(1, NT // 2) as i:
                scale_x(i, 0)
                scale_x(i, 1)
            act.wait_ge(bias_raw_in, 48)
            act.activation(bias_top.bitcast(F32R), bias_all, ACT.Copy).then_inc(bias_hi, 1)
            for c in range(2):
                act.wait_ge(cproj_done, c + 1)
                act.activation(PT[c][:], banks(4 * c + 2, 2), ACT.Sigmoid).then_inc(sig_ready, 1)
            act.wait_ge(angle_step, 16)
            act.activation(sinT[:], S[1][:], ACT.Sin).then_inc(trig_ready, 1)
            act.activation(cosT[:], S[2][:], ACT.Sin).then_inc(trig_ready, 1)
            act.wait_ge(zeros_set, 1)
            reps = MAX_BLOCKS * D // 256
            act.dma_start(y_dram.rearrange("(p r) (c n) -> p (r c) n", p=P, n=256),
                          zeros[:].unsqueeze(1).to_broadcast([P, reps, 256])).then_inc(rows_zero, 16)

            with act.Fori(0, PAIRS) as g:
                for m in range(2):
                    act.wait_ge(proj_done, 3 * g + m + 1)
                    act.wait_ge(qk_ready, 2 * g + m)
                    act.activation(qraw[:], banks(2 * m, 2), ACT.Copy,
                                   scale=HD ** -0.5 if m == 0 else 1.0).then_inc(raw_ready, 1)
                    if m == 0:
                        act.wait_ge(proj_done, 3 * g + 3)
                        act.activation(vT[:], banks(4, 2), ACT.Copy).then_inc(vt_ready, 1)
                act.wait_ge(vtr_done, g + 1)
                act.activation(V[:].rearrange("p t c -> p (t c)"), banks(2, 2), ACT.Copy).then_inc(v_ready, 1)

                def exp(u):
                    n = (u // 2 + 1) * P
                    act.wait_ge(negmax, 16 * g + u + 1)
                    act.activation(S[u % 3][:, 0:n], S[u % 3][:, 0:n], ACT.Exp, bias=stat[:, 32 + u % 4:33 + u % 4],
                                   accum_out=stat[:, 36 + u % 4:37 + u % 4]).then_inc(exp_done, 1)

                def probs(u):
                    n = min((u // 2 + 1) * P, 512)
                    act.wait_ge(pt_done, 16 * g + u + 1)
                    if u >= 2:
                        act.wait_ge(pv_done, 16 * g + u - 1)
                    act.activation(PT[u % 2][:, 0:n], banks(4)[:, 0:n], ACT.Copy).then_inc(pt_act, 1)

                def mix(i):
                    act.wait_ge(ot_done, NT * g + i + 1)
                    act.activation(mixT[:, bass.ds(g, 1), i * P:i * P + P].rearrange("p g n -> p (g n)"),
                                   banks(7)[:, 0:P], ACT.Copy).then_inc(mix_ready, 1)

                exp(0)
                for u in range(16):
                    if u + 1 < 16:
                        exp(u + 1)
                    probs(u)
                    if u >= 4 and u % 2 == 0:
                        mix(u // 2 - 2)
                mix(6)
                mix(7)

            act.wait_ge(ln_dve, 3)
            for c in range(2):
                act.activation(S[c][:], conv[:, c], ACT.Square).then_inc(ln_act, 1)
            act.wait_ge(ln_dve, 5)
            act.activation(PT[0][:], PT[1][:], ACT.Sqrt).then_inc(ln_act, 1)
            for c in range(2):
                act.wait_ge(ln_dve, 7 + 2 * c)
                act.activation(S[c][:], conv[:, c], ACT.Sigmoid).then_inc(ln_act, 1)
            act.wait_ge(ln_act, 5)
            act.activation(PT[0][:, 0:1], PT[1][:, 0:1], ACT.Copy).then_inc(stage2_end, 1)
            act.wait_ge(stage2_end, 4)

            def stage_mix(i, s):
                t = 2 * i + s
                if not (isinstance(i, int) and i == 0):
                    act.wait_ge(out_done, t - 1)
                act.activation(mixS[s][:], mixT[:, :, bass.ds(t * P, P)], ACT.Copy).then_inc(stage_a, 1)

            def norms(i, s):
                t = 2 * i + s
                act.wait_ge(out_done, t + 1)
                act.wait_ge(a3, 4 * t)
                act.activation(junk3[:], banks(2 * s, 2), ACT.Square, accum_out=st3[:, s, 0:1]).then_inc(a3, 1)
                act.wait_ge(d3, D3 * t + 2)
                act.activation(st3[:, s, 2:3], st3[:, s, 1:2], ACT.Sqrt).then_inc(a3, 1)
                act.wait_ge(a3, 4 * t + 2)
                act.wait_ge(d3, D3 * t + 4)
                act.activation(junk3[:], h1[s][:], ACT.Square, accum_out=st3[:, s, 3:4]).then_inc(a3, 1)
                act.wait_ge(d3, D3 * t + 6)
                act.activation(st3[:, s, 5:6], st3[:, s, 4:5], ACT.Sqrt).then_inc(a3, 1)
                act.wait_ge(u2t_done, t + 1)
                act.activation(u2T[:].rearrange("p k n -> p (k n)"), banks(4, 2), ACT.Copy).then_inc(u2t_ready, 1)

            stage_mix(0, 0)
            stage_mix(0, 1)
            with act.Fori(0, NT // 2 - 1) as i:
                norms(i, 0)
                stage_mix(i + 1, 0)
                norms(i, 1)
                stage_mix(i + 1, 1)
            norms(NT // 2 - 1, 0)
            norms(NT // 2 - 1, 1)
            act.wait_ge(g3, 1)
            act.activation(gtmp[:], gate[:], ACT.Exp).then_inc(g3, 1)
            act.wait_ge(e3, TABLE_STEP)
            act.activation(junk3[:, 0:1], junk3[:, 1:2], ACT.Copy).then_inc(stage3_end, 1)
            act.wait_ge(stage3_end, 4)
            act.wait_ge(tab_in, 16)
            act.wait_ge(rows_zero, 16)

            def split_hi(n, c):
                act.wait_ge(raw_in[c % RAW], raw_value(n, c))
                act.wait_ge(w_free, PIECES * n + c + 1)
                act.activation(whi[:, c % SPLIT], raw[:, c % RAW], ACT.Copy).then_inc(hi_ready, 1)

            def columns(b, k):
                act.wait_ge(xt4_done[b], k + 1)
                act.activation(xhi[:, b].rearrange("p k n -> p (k n)"), banks(4, 2), ACT.Copy).then_inc(xhi_ready[b], 1)

            def sigmoid(b, j, k):
                act.wait_ge(gat_ready[b], 4 * k + j + 1)
                act.activation(sig[:, b], gat[:, b], ACT.Sigmoid, scale=ALPHA).then_inc(sig_done[b], 1)

            def hidden(b, j, k):
                act.wait_ge(ht_done[b], 4 * k + j + 1)
                act.activation(hhi[:, b, 2 * j:2 * j + 2].rearrange("p k n -> p (k n)"), banks(6 + b)[:, 0:256],
                               ACT.Copy).then_inc(hhi_ready[b], 1)

            def rows_out(n, row, b, d, k):
                if b == 1:
                    act.wait_ge(y_done, 2 * k + d + 1)
                else:
                    act.wait_ge(w_free, PIECES * n + SPLIT + 11 + d)
                if d == 0:
                    act.wait_ge(y_out[b], 16 * k)
                act.activation(ysb[:, b, d * 512:d * 512 + 512], banks(2 * b + d), ACT.Copy).then_inc(y_used[b][d], 1)
                if d == 1:
                    act.wait_ge(y_used[b][1], k + 1)
                    act.dma_start(y_dram[bass.ds(row + b * P, P), :], ysb[:, b]).then_inc(y_out[b], 16)

            for c in range(SPLIT):
                split_hi(0, c)
            columns(0, 0)
            with act.If(read(act, 0, TWO) > 0):
                columns(1, 0)
            with act.Fori(0, MAX_ITEMS) as n:
                with act.If(read(act, n, LIVE) > 0):
                    two = read(act, n, TWO)
                    k1 = read(act, n, NTWO)
                    nxt = read(act, n + 1, LIVE)
                    nxt2 = read(act, n + 1, TWO)
                    nk1 = read(act, n + 1, NTWO)
                    row = read(act, n, YROW)
                    for c in range(PIECES):
                        j = (c - 1) // 2
                        if c in (1, 3, 5, 7):
                            with act.If(two > 0):
                                sigmoid(1, j, k1)
                            sigmoid(0, j, n)
                        if c in (4, 6, 8, 9):
                            with act.If(two > 0):
                                hidden(1, (c - 3) // 2, k1)
                            hidden(0, (c - 3) // 2, n)
                        if c == 11:
                            for d in range(2):
                                with act.If(two > 0):
                                    rows_out(n, row, 1, d, k1)
                                rows_out(n, row, 0, d, n)
                        if c + SPLIT < PIECES:
                            split_hi(n, c + SPLIT)
                        else:
                            if c == 10:
                                with act.If(nxt2 > 0):
                                    columns(1, nk1)
                            with act.If(nxt > 0):
                                if c == 8:
                                    columns(0, n + 1)
                                split_hi(n + 1, c + SPLIT - PIECES)
            stored = [read(act, P - 1, what) * 16 for what in (BEFORE, NTWO)]
            for b in range(2):
                act.wait_ge(y_out[b], stored[b])
            act_fin(act)

        @block.vector
        def _(dve):
            dve.wait_ge(x_stat, NT)
            dve.tensor_scalar(stat[:, 24:32], stat[:, 0:8], 1.0 / D, EPS, ALU.mult, ALU.add).then_inc(x_var, 1)
            dve.wait_ge(x_var, 1)
            dve.reciprocal(stat[:, 16:24], stat[:, 24:32]).then_inc(x_var, 1)
            dve.wait_ge(cst_in, 16)
            dve.wait_ge(vec_in, 32)

            def columns_x(i, s, last=False):
                t = 2 * i + s
                dve.wait_ge(xt_done, t + 1)
                dve.tensor_tensor(uT[:, :, bass.ds(t * P, P)],
                                  banks(2 * s, 2).rearrange("p (k n) -> p k n", k=KD),
                                  gpre[:].unsqueeze(2).to_broadcast([P, KD, P]), ALU.mult).then_inc(ut_ready, 1)

            with dve.Fori(0, NT // 2) as i:
                columns_x(i, 0)
                columns_x(i, 1)

            a = Count()
            pos, ang, rs, rc, kk = S[0], vT, S[1], S[2], qT
            dve.tensor_copy(kT[:], pos[:].bitcast(I32)).then_inc(angle_step, 1)
            dve.wait_ge(angle_step, a.up())
            dve.tensor_scalar(ang[:], kT[:], freq, None, ALU.mult).then_inc(angle_step, 1)
            dve.wait_ge(angle_step, a.up())
            for turn, dst in ((0.0, rs), (0.25, rc)):
                dve.tensor_scalar(kk[:], ang[:], 1.0 / TWO_PI, turn, ALU.mult, ALU.add).then_inc(angle_step, 1)
                dve.wait_ge(angle_step, a.up())
                dve.tensor_scalar(kk[:], kk[:], ROUND, ROUND, ALU.add, ALU.subtract).then_inc(angle_step, 1)
                dve.wait_ge(angle_step, a.up())
                dve.scalar_tensor_tensor(out=dst[:], in0=kk[:], scalar=-C1, in1=ang[:], op0=ALU.mult,
                                         op1=ALU.add).then_inc(angle_step, 1)
                dve.wait_ge(angle_step, a.up())
                dve.scalar_tensor_tensor(out=dst[:], in0=kk[:], scalar=-C2, in1=dst[:], op0=ALU.mult,
                                         op1=ALU.add).then_inc(angle_step, 1)
                dve.wait_ge(angle_step, a.up())
                dve.scalar_tensor_tensor(out=dst[:], in0=kk[:], scalar=-C3, in1=dst[:], op0=ALU.mult,
                                         op1=ALU.add).then_inc(angle_step, 1)
                dve.wait_ge(angle_step, a.up())
                dve.tensor_scalar(dst[:], dst[:], turn * TWO_PI, PI_IN, ALU.add, ALU.min).then_inc(angle_step, 1)
                dve.wait_ge(angle_step, a.up())
            dve.tensor_scalar(rs[:], rs[:], -PI_IN, None, ALU.max).then_inc(angle_step, 1)
            dve.tensor_scalar(rc[:], rc[:], -PI_IN, None, ALU.max).then_inc(angle_step, 1)

            dve.wait_ge(bias_hi, 1)
            dve.tensor_tensor(bias_all, bias_all, bias_top, ALU.subtract).then_inc(bias_lo, 1)
            dve.wait_ge(glu_pad, 1)
            dve.wait_ge(tables_in, 16)
            dve.wait_ge(taps_in, 80)
            for c in range(2):
                dve.wait_ge(sig_ready, c + 1)
                dve.tensor_tensor(glu[:, c, TAPS - 1:], banks(4 * c, 2), PT[c][:], ALU.mult).then_inc(glu_ready, 1)
            for c in range(2):
                dve.wait_ge(glu_ready, c + 1)
                dve.tensor_scalar(conv[:, c], glu[:, c, TAPS - 1:], wdw[:, c, TAPS - 1:TAPS], cvec[:, 0, c:c + 1],
                                  ALU.mult, ALU.add).then_inc(conv_step, 1)

            with dve.Fori(0, PAIRS) as g:
                for j in range(TAPS_PER_PAIR):
                    for c in range(2):
                        dve.wait_ge(conv_step, 2 * TAPS_PER_PAIR * g + 2 * j + c + 1)
                        tap = TAPS_PER_PAIR * g + j
                        dve.scalar_tensor_tensor(out=conv[:, c], in0=glu[:, c, bass.ds(tap, T)],
                                                 scalar=wdw[:, c, bass.ds(tap, 1)], in1=conv[:, c],
                                                 op0=ALU.mult, op1=ALU.add).then_inc(conv_step, 1)
                for m in range(2):
                    dst = qT if m == 0 else kT
                    b = 6 if m == 0 else 0
                    dve.wait_ge(rot_done, 2 * g + m + 1)
                    dve.wait_ge(trig_ready, 2)
                    dve.tensor_tensor(dst[:], banks(b, 2), sinT[:], ALU.mult).then_inc(rot_step, 1)
                    dve.wait_ge(rot_step, 2 * g + m + 1)
                    dve.wait_ge(cos_part, 2 * g + m + 1)
                    dve.tensor_tensor(dst[:], dst[:], rotc[:], ALU.add).then_inc(qk_ready, 1)

                def mask_max(u):
                    i = u // 2
                    n = (i + 1) * P
                    dve.wait_ge(s_done, 16 * g + u + 1)
                    hold(dve, pt_done, 16 * g + max(u - 2, 0))
                    mx = stat[:, 40 + u % 4:41 + u % 4]
                    dve.tensor_tensor_reduce(out=S[u % 3][:, 0:n], in0=banks(2 * (u % 2), 2)[:, 0:n],
                                             in1=mlog[:, T - n:T], scale=1.0, scalar=NEG, op0=ALU.add, op1=ALU.max,
                                             accum_out=mx).then_inc(mask_done, 1)
                    dve.wait_ge(mask_done, 16 * g + u + 1)
                    dve.tensor_scalar(stat[:, 32 + u % 4:33 + u % 4], mx, -1.0, None, ALU.mult).then_inc(negmax, 1)

                def output(u):
                    i, hd = u // 2, u % 2
                    dve.wait_ge(exp_done, 16 * g + u + 1)
                    rd = stat[:, 44 + u % 4:45 + u % 4]
                    dve.reciprocal(rd, stat[:, 36 + u % 4:37 + u % 4]).then_inc(rden_done, 1)
                    dve.wait_ge(rden_done, 16 * g + u + 1)
                    dve.wait_ge(pv_done, 16 * g + u + 1)
                    if i >= 2:
                        dve.wait_ge(ot_done, NT * g + i - 1)
                    dve.tensor_scalar(o_sb[:, i % 2, hd * HD:hd * HD + HD], banks(6)[:, 0:HD], rd, None,
                                      ALU.mult).then_inc(o_ready, 1)

                mask_max(0)
                mask_max(1)
                for u in range(16):
                    if u + 2 < 16:
                        mask_max(u + 2)
                    if u >= 8:
                        n = (u // 2 + 1) * P
                        dve.wait_ge(pt_done, 16 * g + u + 1)
                        dve.wait_ge(pv_done, 16 * g + u - 1)
                        dve.tensor_copy(PT[u % 2][:, 512:n], banks(5)[:, 0:n - 512]).then_inc(pt_dve, 1)
                    if u >= 1:
                        output(u - 1)
                output(15)

            n = Count()
            dve.wait_ge(conv_step, 2 * TAPS)
            dve.tensor_copy(stat[:, 48:49], stat[:, 40:41]).then_inc(ln_dve, 1)
            n.up()
            dve.wait_ge(ln_pe, 1)
            for c in range(2):
                dve.scalar_tensor_tensor(out=conv[:, c], in0=banks(0, 2), scalar=-1.0 / CC, in1=conv[:, c],
                                         op0=ALU.mult, op1=ALU.add).then_inc(ln_dve, 1)
                n.up()
            dve.wait_ge(ln_pe, 2)
            dve.tensor_scalar(PT[1][:], banks(2, 2), 1.0 / CC, EPS, ALU.mult, ALU.add).then_inc(ln_dve, 1)
            dve.wait_ge(ln_dve, n.up())
            dve.reciprocal(PT[1][:], PT[1][:]).then_inc(ln_dve, 1)
            n.up()
            dve.wait_ge(ln_act, 3)
            for c in range(2):
                dve.tensor_tensor(conv[:, c], conv[:, c], PT[0][:], ALU.mult).then_inc(ln_dve, 1)
                dve.wait_ge(ln_dve, n.up())
                dve.tensor_scalar(conv[:, c], conv[:, c], cvec[:, 1, c:c + 1], cvec[:, 2, c:c + 1],
                                  ALU.mult, ALU.add).then_inc(ln_dve, 1)
                n.up()
            for c in range(2):
                dve.wait_ge(ln_act, 4 + c)
                dve.tensor_tensor(mixT[:, PAIRS + c], conv[:, c], S[c][:], ALU.mult).then_inc(ln_dve, 1)
                dve.wait_ge(ln_dve, n.up())
            dve.wait_ge(mix_ready, NT * PAIRS)
            dve.tensor_copy(stat[:, 50:51], stat[:, 48:49]).then_inc(stage2_end, 1)
            dve.wait_ge(stage2_end, 4)

            dve.wait_ge(vec3_in, 64)
            dve.memset(Macc[:], 0.0).then_inc(e3, 1)
            e = Count()
            dve.wait_ge(e3, e.up())

            def tile3(i, s):
                t = 2 * i + s
                n = Count(D3 * t)
                if not (isinstance(i, int) and i == 0):
                    dve.wait_ge(h1_out[s], 16 * i)
                    dve.wait_ge(u2_out[s], 16 * i)
                dve.wait_ge(a3, 4 * t + 1)
                dve.tensor_scalar(st3[:, s, 1:2], st3[:, s, 0:1], 1.0 / D, EPS, ALU.mult, ALU.add).then_inc(d3, 1)
                dve.wait_ge(d3, n.up())
                dve.reciprocal(st3[:, s, 1:2], st3[:, s, 1:2]).then_inc(d3, 1)
                n.up()
                dve.wait_ge(a3, 4 * t + 2)
                dve.scalar_tensor_tensor(out=h1[s][:], in0=banks(2 * s, 2), scalar=st3[:, s, 2:3], in1=gpost[:],
                                         op0=ALU.mult, op1=ALU.mult).then_inc(d3, 1)
                dve.wait_ge(d3, n.up())
                dve.wait_ge(xr_in[s], 16 * i + 16)
                dve.tensor_tensor(h1[s][:], h1[s][:], xr[s][:], ALU.add).then_inc(d3, 1)
                n.up()
                dve.wait_ge(a3, 4 * t + 3)
                dve.tensor_scalar(st3[:, s, 4:5], st3[:, s, 3:4], 1.0 / D, EPS, ALU.mult, ALU.add).then_inc(d3, 1)
                dve.wait_ge(d3, n.up())
                dve.reciprocal(st3[:, s, 4:5], st3[:, s, 4:5]).then_inc(d3, 1)
                n.up()
                dve.wait_ge(a3, 4 * t + 4)
                dve.scalar_tensor_tensor(out=u2[s][:], in0=h1[s][:], scalar=st3[:, s, 5:6], in1=gffn[:],
                                         op0=ALU.mult, op1=ALU.mult).then_inc(d3, 1)
                n.up()
                dve.wait_ge(logit_done, t + 1)
                dve.tensor_tensor(logit[:], banks(6)[:, 0:E], br[:], ALU.add).then_inc(d3, 1)
                hold(dve, d3, n.up())
                dve.max(top8[:], logit[:]).then_inc(d3, 1)
                hold(dve, d3, n.up())
                dve.max_index(topi[:], top8[:], logit[:]).then_inc(d3, 1)
                dve.wait_ge(d3, n.up())
                dve.tensor_copy(topf[:], topi[:]).then_inc(d3, 1)
                dve.wait_ge(d3, n.up())
                for k in range(TOPK):
                    dve.tensor_scalar(hot[:, k], iota_e, topf[:, k:k + 1], None, ALU.is_equal).then_inc(d3, 1)
                dve.wait_ge(d3, n.up(TOPK))
                dve.tensor_tensor(junk32[:, 0:2], hot[:, 0:2], hot[:, 2:4], ALU.add).then_inc(d3, 1)
                dve.wait_ge(d3, n.up())
                dve.tensor_tensor(M[:], junk32[:, 0], junk32[:, 1], ALU.add).then_inc(d3, 1)
                dve.wait_ge(d3, n.up())
                dve.wait_ge(rank_done, t + 1)
                for k in range(TOPK):
                    dve.tensor_tensor(junk32[:, k], hot[:, k], banks(7)[:, 0:E], ALU.mult).then_inc(d3, 1)
                    n.up()
                dve.wait_ge(d3, n.up(0))
                dve.tensor_reduce(rank[:], junk32[:], mybir.AxisListType.X, ALU.add).then_inc(d3, 1)
                dve.wait_ge(d3, n.up())
                dve.scalar_tensor_tensor(out=rowf[:], in0=topf[:, 0:TOPK], scalar=float(T), in1=rank[:],
                                         op0=ALU.mult, op1=ALU.add).then_inc(d3, 1)
                dve.wait_ge(d3, n.up())
                dve.wait_ge(ids_out, 16 * TOPK * t)
                dve.tensor_copy(row_i[:], rowf[:]).then_inc(d3, 1)
                n.up()
                dve.tensor_copy(idx_all[:, bass.ds(t, 1)].rearrange("p t k -> p (t k)"), topf[:, 0:TOPK]).then_inc(d3, 1)
                n.up()
                dve.tensor_copy(rank_all[:, bass.ds(t, 1)].rearrange("p t k -> p (t k)"), rank[:]).then_inc(d3, 1)
                n.up()
                dve.tensor_tensor(Macc[:], Macc[:], M[:], ALU.add).then_inc(d3, 1)
                n.up()
                dve.tensor_copy(top[:, bass.ds(t, 1)].rearrange("p t k -> p (t k)"), top8[:]).then_inc(d3, 1)
                n.up()
                dve.tensor_copy(tid_i[:], tid_f[:]).then_inc(d3, 1)
                dve.wait_ge(d3, n.up())
                dve.tensor_scalar(tid_f[:], tid_f[:], float(P), None, ALU.add).then_inc(d3, 1)
                assert n.up() is not None and n.n == D3, n.n

            dve.tensor_copy(tid_f[:], pidx).then_inc(e3, 1)
            dve.wait_ge(e3, e.up())
            with dve.Fori(0, NT // 2) as i:
                tile3(i, 0)
                tile3(i, 1)
            dve.wait_ge(d3, D3 * NT)
            dve.tensor_tensor(gate[:], top[:, :, 0:TOPK], top[:, :, 0:1].to_broadcast([P, NT, TOPK]),
                              ALU.subtract).then_inc(g3, 1)

            def step(ins):
                ins.then_inc(e3, 1)
                dve.wait_ge(e3, e.up())

            dve.wait_ge(cnt_done, 1)
            step(dve.tensor_copy(cnt[:], banks(0)[:, 0:E]))
            step(dve.tensor_scalar(npass[:], cnt[:], float(BLK), 1.0, ALU.is_gt, ALU.add))
            for q in (2, 3):
                step(dve.scalar_tensor_tensor(out=npass[:], in0=cnt[:], scalar=float(q * BLK), in1=npass[:],
                                              op0=ALU.is_gt, op1=ALU.add))
            step(dve.tensor_scalar(nblk[:], cnt[:], float(P), 1.0, ALU.is_gt, ALU.add))
            for q in range(2, T // P):
                step(dve.scalar_tensor_tensor(out=nblk[:], in0=cnt[:], scalar=float(q * P), in1=nblk[:],
                                              op0=ALU.is_gt, op1=ALU.add))
            step(dve.tensor_copy(pref[:, 0, 0], npass[:]))
            step(dve.tensor_copy(pref[:, 0, 1], nblk[:]))
            cur = 0
            for sh in (1, 2, 4, 8, 16):
                step(dve.tensor_copy(pref[:, 1 - cur, :, 0:sh], pref[:, cur, :, 0:sh]))
                step(dve.tensor_tensor(pref[:, 1 - cur, :, sh:E], pref[:, cur, :, sh:E], pref[:, cur, :, 0:E - sh],
                                       ALU.add))
                cur = 1 - cur
            step(dve.tensor_scalar(hot[:, 0], pref[:, cur, 0], pidx, None, ALU.is_le))
            step(dve.memset(hot[:, 1], 1.0))
            step(dve.tensor_tensor_reduce(out=hot[:, 2], in0=hot[:, 0], in1=hot[:, 1], scale=1.0, scalar=0.0,
                                          op0=ALU.mult, op1=ALU.add, accum_out=item[:, EXPERT:EXPERT + 1]))
            step(dve.tensor_tensor_reduce(out=hot[:, 2], in0=hot[:, 0], in1=npass[:], scale=1.0, scalar=0.0,
                                          op0=ALU.mult, op1=ALU.add, accum_out=item[:, BEFORE:BEFORE + 1]))
            step(dve.tensor_tensor(item[:, START:START + 1], pidx, item[:, BEFORE:BEFORE + 1], ALU.subtract))
            step(dve.tensor_scalar(item[:, START:START + 1], item[:, START:START + 1], float(BLK), None, ALU.mult))
            step(dve.tensor_scalar(hot[:, 0], iota_e, item[:, EXPERT:EXPERT + 1], None, ALU.is_equal))
            step(dve.tensor_tensor_reduce(out=hot[:, 2], in0=hot[:, 0], in1=cnt[:], scale=1.0, scalar=0.0,
                                          op0=ALU.mult, op1=ALU.add, accum_out=item[:, YROW:YROW + 1]))
            step(dve.tensor_tensor(item[:, YROW:YROW + 1], item[:, YROW:YROW + 1], item[:, START:START + 1], ALU.subtract))
            step(dve.scalar_tensor_tensor(out=item[:, ROW:ROW + 1], in0=item[:, EXPERT:EXPERT + 1], scalar=float(T),
                                          in1=item[:, START:START + 1], op0=ALU.mult, op1=ALU.add))
            step(dve.tensor_scalar(item[:, LIVE:LIVE + 1], item[:, EXPERT:EXPERT + 1], float(E), None, ALU.is_lt))
            step(dve.tensor_scalar(item[:, TWO:TWO + 1], item[:, YROW:YROW + 1], float(P), None, ALU.is_gt))
            two_at = e.up(0)
            dve.wait_ge(n2_done, 1)
            step(dve.tensor_copy(item[:, NTWO:NTWO + 1], banks(1)[:, 0:1]))
            step(dve.tensor_tensor(first[:], pref[:, cur, 1], nblk[:], ALU.subtract))
            step(dve.tensor_scalar(first[:], first[:], float(P), None, ALU.mult))
            step(dve.tensor_tensor_reduce(out=hot[:, 2], in0=hot[:, 0], in1=first[:], scale=1.0, scalar=0.0,
                                          op0=ALU.mult, op1=ALU.add, accum_out=item[:, YROW:YROW + 1]))
            step(dve.tensor_tensor(item[:, YROW:YROW + 1], item[:, YROW:YROW + 1], item[:, START:START + 1], ALU.add))
            step(dve.tensor_copy(item_i[:], item[:]))
            row_t = idx_all[:].rearrange("p t k -> p (t k)").unsqueeze(2).to_broadcast([P, NT * TOPK, E])
            step(dve.tensor_tensor(hot_all[:], row_t, iota_e.unsqueeze(1).to_broadcast([P, NT * TOPK, E]), ALU.is_equal))
            step(dve.tensor_tensor(hot_all[:], hot_all[:], first[:].unsqueeze(1).to_broadcast([P, NT * TOPK, E]),
                                   ALU.mult))
            step(dve.tensor_reduce(idx_all[:].rearrange("p t k -> p (t k)"), hot_all[:], mybir.AxisListType.X, ALU.add))
            step(dve.tensor_tensor(row_of[:], idx_all[:], rank_all[:], ALU.add))
            assert two_at == TWO_STEP and e.n == TABLE_STEP + 4, (two_at, e.n)
            dve.wait_ge(g3, 2)
            dve.tensor_reduce(gsum[:], gtmp[:], mybir.AxisListType.X, ALU.add).then_inc(g3, 1)
            dve.wait_ge(g3, 3)
            dve.reciprocal(gsum[:], gsum[:]).then_inc(g3, 1)
            dve.wait_ge(g3, 4)
            dve.tensor_tensor(gate[:], gtmp[:], gsum[:].unsqueeze(2).to_broadcast([P, NT, TOPK]),
                              ALU.mult).then_inc(g3, 1)
            dve.wait_ge(g3, 5)
            dve.tensor_copy(gsum[:, 0:1], gtmp[:, 0, 0:1]).then_inc(stage3_end, 1)
            dve.wait_ge(stage3_end, 4)
            dve.wait_ge(tab_in, 16)
            experts_dve(dve)
            out_dve(dve)

_INS = ['x', 'p', 'positions', 'g_mix_pre', 'w_in', 'w_dw', 'b_dw', 'g_conv_ln', 'b_conv_ln', 'w_out', 'g_mix_post',
        'g_ffn_pre', 'w_router', 'b_router', 'w_gate_up', 'b_gate_up', 'w_down', 'b_down', 'g_ffn_post', 'w_ple',
        'w_ple_gate', 'g_ple_post']
_BRANCHES = ((128, 1), (512, 4), (2048, 16))
_ROPE_THETA, _ROPE_DIM = 500000.0, HD // 4


def _tables():
    import numpy as np
    c = np.zeros((P, 424), np.float32)
    c[:, 0:128] = np.eye(P)
    half = _ROPE_DIM // 2
    inv = (_ROPE_THETA ** (-np.arange(0, _ROPE_DIM, 2) / _ROPE_DIM)).astype(np.float32)
    for h in (0, HD):
        for d in range(half):
            c[h + half + d, 128 + h + d] = -1.0
            c[h + d, 128 + h + half + d] = 1.0
            c[h + d, 416] = c[h + half + d, 416] = inv[d]
    k, m = np.meshgrid(np.arange(P), np.arange(P), indexing="ij")
    c[:, 256:384] = k < m
    c[:, 384:416] = np.arange(E)
    c[:, 417] = np.arange(P)
    dist = np.arange(P)[:, None] + (T - P) - np.arange(T)[None, :]
    times = sum(((dist >= 0) & (dist % dil == 0) & (dist <= win)).astype(np.int32) for win, dil in _BRANCHES)
    logs = np.where(times > 0, np.log(np.maximum(times, 1)), NEG).astype(np.float32)
    return c, logs


def kernel(**inputs):
    import numpy as _np
    import concourse.bacc as _bacc
    from concourse import mybir as _mybir
    from concourse.bass_utils import run_bass_kernel_spmd as _run

    nc = _bacc.Bacc("TRN2", target_bir_lowering=False, num_devices=1)
    arrays, args = {}, []

    def give(name, a):
        arrays[f"in_{name}_dram"] = a
        args.append(nc.dram_tensor(f"in_{name}_dram", a.shape, _mybir.dt.from_np(a.dtype), kind="ExternalInput").ap())

    for name in _INS:
        give(name, _np.ascontiguousarray(inputs[name]))
    for name, a in zip(("consts", "mult_log"), _tables()):
        give(name, a)
    args.append(nc.dram_tensor("out_0_dram", (1, T, D), _mybir.dt.float32, kind="ExternalOutput").ap())
    layer(nc, *args)
    r = _run(nc, [arrays], core_ids=[0])
    return r.results[0]["out_0_dram"]
```
